# Optimizing a Trainium2 kernel written in Bass

```python
import math
import jax, jax.numpy as jnp
from jax import lax
import numpy as np

D_MODEL = 2048
BATCH = 1
SEQ = 256
DEPTH = 1

GRID_W = 64
CTX_LEN = 256
D_MIX = D_MODEL
GDN_HEADS = 8
GDN_DK = 128
GDN_DV = 128
GDN_W = GDN_HEADS * GDN_DV
FOURIER_W = D_MIX - GDN_W
FOURIER_GROUPS = 8
FOURIER_GC = FOURIER_W // FOURIER_GROUPS
CONV_K = 5
CHUNK = 64
D_FF = 5632
N_MOD = 9
RMS_EPS = 1e-6
L2_EPS = 1e-6
DT_MIN = 1e-3
DT_MAX = 1e-1
P_IN = 4 * GDN_W + 4 * GDN_HEADS + FOURIER_W

kernel_name = 'hybrid_gdn_fnet_macaron_prefix'

def rmsnorm(x, g):
    xf = x.astype(jnp.float32)
    y = xf * lax.rsqrt(jnp.mean(xf * xf, axis=-1, keepdims=True) + RMS_EPS)
    return (y * g.astype(jnp.float32)).astype(x.dtype)

def l2norm(x):
    return x * lax.rsqrt(jnp.sum(x * x, axis=-1, keepdims=True) + L2_EPS)

def pre(x, mod, i, g):
    return rmsnorm(x, g) * (1.0 + mod[3 * i + 1]) + mod[3 * i]

def post(x, y, mod, i, g, res_w):
    return x + res_w * mod[3 * i + 2] * rmsnorm(y, g)

def swiglu(h, w_gate, w_up, w_down):
    return (jax.nn.silu(h @ w_gate) * (h @ w_up)) @ w_down

def dwconv(u, w):
    pad = CONV_K // 2
    return lax.conv_general_dilated(
        u, w[:, None, :].astype(u.dtype), window_strides=(1,), padding=[(pad, pad)],
        dimension_numbers=('NWC', 'WIO', 'NWC'), feature_group_count=u.shape[-1])

def conv_rows(u, w):
    b, l, ch = u.shape
    rows = l // GRID_W
    return dwconv(u.reshape(b * rows, GRID_W, ch), w).reshape(b, l, ch)

def mixer_inputs(h, w_in, conv_w, a_log, dt_bias, conv_fn):
    b, l, _ = h.shape
    hh = GDN_HEADS
    p = h @ w_in
    qkv = jax.nn.silu(conv_fn(p[..., :3 * GDN_W], conv_w))
    z = p[..., 3 * GDN_W:4 * GDN_W]
    a = p[..., 4 * GDN_W:4 * GDN_W + 2 * hh].reshape(b, l, 2, hh).astype(jnp.float32)
    bb = p[..., 4 * GDN_W + 2 * hh:4 * GDN_W + 4 * hh].reshape(b, l, 2, hh).astype(jnp.float32)
    f = p[..., 4 * GDN_W + 4 * hh:]
    heads = lambda t: t.reshape(b, l, hh, -1).transpose(0, 2, 1, 3).astype(jnp.float32)
    q = heads(qkv[..., :GDN_W])
    k = heads(qkv[..., GDN_W:2 * GDN_W])
    v = heads(qkv[..., 2 * GDN_W:])
    q = l2norm(q) * (GDN_DK ** -0.5)
    k = l2norm(k)
    g = -jnp.exp(a_log.astype(jnp.float32)) * jax.nn.softplus(a + dt_bias.astype(jnp.float32))
    g = g.transpose(2, 0, 3, 1)
    beta = jax.nn.sigmoid(bb).transpose(2, 0, 3, 1)
    return q, k, v, beta, g, z, f

def gdn_chunked(q, k, v, beta, g, h0):
    b, hh, l, _ = q.shape
    dv = v.shape[-1]
    n = l // CHUNK
    ch = lambda t: t.reshape(b, hh, n, CHUNK, *t.shape[3:])
    q, k, v, beta, g = ch(q), ch(k), ch(v), ch(beta), ch(g)
    G = jnp.cumsum(g, axis=-1)
    pos = jnp.arange(CHUNK)
    incl = pos[:, None] >= pos[None, :]
    decay = jnp.exp(jnp.where(incl, G[..., :, None] - G[..., None, :], -jnp.inf))
    kk = jnp.einsum('bhnck,bhnmk->bhncm', k, k)
    eye = jnp.eye(CHUNK, dtype=q.dtype)
    a_mat = eye + jnp.where(pos[:, None] > pos[None, :], beta[..., :, None] * decay * kk, 0.0)
    gamma = jnp.exp(G)
    rhs = jnp.concatenate([beta[..., None] * v, (beta * gamma)[..., None] * k], axis=-1)
    sol = lax.linalg.triangular_solve(a_mat, rhs, left_side=True, lower=True, unit_diagonal=True)
    v_t, w = sol[..., :dv], sol[..., dv:]
    p_qk = jnp.einsum('bhnck,bhnmk->bhncm', q, k) * decay
    q_g = q * gamma[..., None]
    k_d = k * jnp.exp(G[..., -1:] - G)[..., None]
    g_last = gamma[..., -1]
    xs = tuple(jnp.moveaxis(t, 2, 0) for t in (q_g, p_qk, v_t, w, k_d, g_last))

    def step(h, xc):
        qg_c, pqk_c, vt_c, w_c, kd_c, gl_c = xc
        u = vt_c - jnp.einsum('bhck,bhkv->bhcv', w_c, h)
        o = jnp.einsum('bhck,bhkv->bhcv', qg_c, h) + jnp.einsum('bhcm,bhmv->bhcv', pqk_c, u)
        h = h * gl_c[..., None, None] + jnp.einsum('bhck,bhcv->bhkv', kd_c, u)
        return h, o

    h_final, o = lax.scan(step, h0, xs)
    return jnp.moveaxis(o, 0, 2).reshape(b, hh, l, dv), h_final

def gdn_bidir(qc, kc, vc, bc, gc, ql, kl, vl, bl, gl):
    b = qc.shape[0]
    outs_c, outs_l = [], []
    for d in range(2):
        flip = (lambda t: jnp.flip(t, axis=2)) if d == 1 else (lambda t: t)
        h0 = jnp.zeros((b, GDN_HEADS, GDN_DK, GDN_DV), jnp.float32)
        o_c, h_c = gdn_chunked(flip(qc), flip(kc), flip(vc), flip(bc[d]), flip(gc[d]), h0)
        o_l, _ = gdn_chunked(flip(ql), flip(kl), flip(vl), flip(bl[d]), flip(gl[d]), h_c)
        outs_c.append(flip(o_c))
        outs_l.append(flip(o_l))
    return outs_c[0] + outs_c[1], outs_l[0] + outs_l[1]

def mixer_output(o, z, f, g_onorm, w_out):
    b, hh, l, dv = o.shape
    o = o.transpose(0, 2, 1, 3)
    zz = z.reshape(b, l, hh, dv).astype(jnp.float32)
    gd = (rmsnorm(o, g_onorm) * jax.nn.silu(zz)).reshape(b, l, GDN_W).astype(z.dtype)
    ff = f.reshape(b, l, FOURIER_GROUPS, FOURIER_GC).astype(jnp.float32)
    fr = jnp.fft.fft2(ff, axes=(1, 3), norm='ortho').real.reshape(b, l, FOURIER_W).astype(z.dtype)
    return jnp.concatenate([gd, fr], axis=-1) @ w_out

def setup_inputs(seed: int = 0) -> dict:
    key = jax.random.key(seed)
    ks = jax.random.split(key, 24)
    f32 = jnp.float32
    nrm = lambda kk, shape, fan: jax.random.normal(kk, shape, f32) * (fan ** -0.5)
    gain = lambda kk, shape: 1.0 + 0.02 * jax.random.normal(kk, shape, f32)
    dt = jnp.exp(jax.random.uniform(ks[14], (DEPTH, 2, GDN_HEADS), f32, math.log(DT_MIN), math.log(DT_MAX)))
    return {
        'x': jax.random.normal(ks[0], (BATCH, SEQ, D_MODEL), f32),
        'c': jax.random.normal(ks[1], (BATCH, D_MODEL), f32),
        'ctx': jax.random.normal(ks[2], (BATCH, CTX_LEN, D_MODEL), f32),
        'c_ctx': jax.random.normal(ks[3], (D_MODEL,), f32),
        'w_mod': 0.5 * nrm(ks[4], (DEPTH, D_MODEL, N_MOD * D_MODEL), D_MODEL),
        'b_mod': 0.02 * jax.random.normal(ks[5], (DEPTH, N_MOD * D_MODEL), f32),
        'g_pre': gain(ks[6], (DEPTH, 3, D_MODEL)),
        'g_post': gain(ks[7], (DEPTH, 3, D_MODEL)),
        'w1_gate': nrm(ks[8], (DEPTH, D_MODEL, D_FF), D_MODEL),
        'w1_up': nrm(ks[9], (DEPTH, D_MODEL, D_FF), D_MODEL),
        'w1_down': nrm(ks[10], (DEPTH, D_FF, D_MODEL), D_FF),
        'w_in': nrm(ks[11], (DEPTH, D_MODEL, P_IN), D_MODEL),
        'conv_w': nrm(ks[12], (DEPTH, CONV_K, 3 * GDN_W), CONV_K),
        'a_log': jnp.log(jax.random.uniform(ks[13], (DEPTH, 2, GDN_HEADS), f32, 1.0, 16.0)),
        'dt_bias': dt + jnp.log(-jnp.expm1(-dt)),
        'g_onorm': gain(ks[15], (DEPTH, GDN_DV)),
        'w_out': nrm(ks[16], (DEPTH, D_MIX, D_MODEL), D_MIX),
        'w2_gate': nrm(ks[17], (DEPTH, D_MODEL, D_FF), D_MODEL),
        'w2_up': nrm(ks[18], (DEPTH, D_MODEL, D_FF), D_MODEL),
        'w2_down': nrm(ks[19], (DEPTH, D_FF, D_MODEL), D_FF),
    }

def reference(x, c, ctx, c_ctx, w_mod, b_mod, g_pre, g_post, w1_gate, w1_up, w1_down,
              w_in, conv_w, a_log, dt_bias, g_onorm, w_out, w2_gate, w2_up, w2_down):
    b = x.shape[0]
    for l in range(DEPTH):
        mod_l = (jax.nn.silu(c) @ w_mod[l] + b_mod[l]).reshape(b, N_MOD, D_MODEL).transpose(1, 0, 2)[:, :, None, :]
        mod_c = (jax.nn.silu(c_ctx) @ w_mod[l] + b_mod[l]).reshape(N_MOD, 1, 1, D_MODEL)
        x = post(x, swiglu(pre(x, mod_l, 0, g_pre[l, 0]), w1_gate[l], w1_up[l], w1_down[l]), mod_l, 0, g_post[l, 0], 0.5)
        ctx = post(ctx, swiglu(pre(ctx, mod_c, 0, g_pre[l, 0]), w1_gate[l], w1_up[l], w1_down[l]), mod_c, 0, g_post[l, 0], 0.5)
        qc, kc, vc, bc, gc, zc, fc = mixer_inputs(pre(ctx, mod_c, 1, g_pre[l, 1]), w_in[l], conv_w[l], a_log[l], dt_bias[l], dwconv)
        ql, kl, vl, bl, gl, zl, fl = mixer_inputs(pre(x, mod_l, 1, g_pre[l, 1]), w_in[l], conv_w[l], a_log[l], dt_bias[l], conv_rows)
        o_c, o_l = gdn_bidir(qc, kc, vc, bc, gc, ql, kl, vl, bl, gl)
        x = post(x, mixer_output(o_l, zl, fl, g_onorm[l], w_out[l]), mod_l, 1, g_post[l, 1], 1.0)
        x = post(x, swiglu(pre(x, mod_l, 2, g_pre[l, 2]), w2_gate[l], w2_up[l], w2_down[l]), mod_l, 2, g_post[l, 2], 0.5)
        if l + 1 < DEPTH:
            ctx = post(ctx, mixer_output(o_c, zc, fc, g_onorm[l], w_out[l]), mod_c, 1, g_post[l, 1], 1.0)
            ctx = post(ctx, swiglu(pre(ctx, mod_c, 2, g_pre[l, 2]), w2_gate[l], w2_up[l], w2_down[l]), mod_c, 2, g_post[l, 2], 0.5)
    return x


_drawn_inputs = setup_inputs


def setup_inputs(seed=0):
    import zlib

    import numpy as np

    out = dict(_drawn_inputs(seed))
    spreads = {}
    factors = {'c_ctx': 3.379, 'g_pre': 5.954, 'g_post': 7.649, 'g_onorm': 8.0}
    for name, (base, spread) in spreads.items():
        noise = np.random.default_rng([zlib.crc32(name.encode()), seed]).standard_normal(out[name].shape)
        drawn = base * np.exp(spread * noise) if base else spread * noise
        out[name] = __import__('jax').numpy.asarray(drawn.astype(out[name].dtype))
    for name, factor in factors.items():
        out[name] = (out[name] * factor).astype(out[name].dtype)
    return out
```

```python
from contextlib import ExitStack

import numpy as np

import concourse.bass as bass
from concourse import mybir

F32 = mybir.dt.float32
F32R = mybir.dt.float32r
ALU = mybir.AluOpType
ACT = mybir.ActivationFunctionType
ds = bass.ds

P = 128
D = 2048
KT = D // P
CTX = 256
SEQ = 256
TOK = CTX + SEQ
DFF = 5632
HEADS = 8
GROUP = 512
ROUNDS = DFF // GROUP
GT = GROUP // P
N_MOD = 9
CHUNK = 64
STEPS = TOK // CHUNK
LSTEPS = SEQ // CHUNK
ROW = 64
TAPS = 5
EPS = 1e-6
RAW_SLOTS = 4
UNIT = 1024
PART_SLOTS = 4

V_CCTX, V_C, V_BMOD, V_GPRE, V_GPOST, N_VEC = 0, 1, 2, 11, 14, 17
K_G, K_BETA, K_BG, K_GAMMA, K_KD, K_LASTF, K_LASTB, N_SC = 0, 1, 2, 3, 4, 5, 6, 7
K_BR2, K_BGR2, K_BR, K_QS, K_GQS, N_HSC = 7, 8, 9, 10, 11, 12

PAT_MOD = "m" * 16
PAT_A = "wmm" * 8 + "w" * 4
PAT_B = "w" * 12
PAT_IN = "w" * 4
A_ROUNDS = 7


class Segment:

    def __init__(self, before, iters, pattern):
        self.pos = before.pos + before.iters * len(before.pattern) if before else 0
        self.weight = before.weight + before.iters * before.pattern.count("w") if before else 0
        self.iters, self.pattern = iters, pattern
        self.at = [n for n, c in enumerate(pattern) if c == "w"]
        self.mods = [n for n, c in enumerate(pattern) if c == "m"]


S_MOD = Segment(None, 2, PAT_MOD)
S_A = Segment(S_MOD, A_ROUNDS, PAT_A)
S_B = Segment(S_A, ROUNDS - A_ROUNDS, PAT_B)
S_KV = Segment(S_B, 4, PAT_IN)
S_Q = Segment(S_KV, 2, PAT_IN)
S_Z = Segment(S_Q, 2, PAT_IN)
S_F = Segment(S_Z, 2, PAT_IN)
S_AB = Segment(S_F, 1, "w")
S_OUT = Segment(S_AB, 4, PAT_IN)
S_F2 = Segment(S_OUT, ROUNDS - 1, PAT_B)
S_F2L = Segment(S_F2, 1, PAT_B)

N_FULL = 11
N_PAIR = 3
C2_COLS = N_FULL * P + N_PAIR * CHUNK + 2 * P + 4 * SEQ


def shape_constants():
    c1 = np.concatenate([np.eye(P), np.ones((P, P))], 1).astype(np.float32)
    m, i = np.meshgrid(np.arange(P), np.arange(P), indexing="ij")
    same = m // CHUNK == i // CHUNK
    fwd = m < CHUNK
    incl = same & np.where(fwd, m <= i, m >= i)
    strict = same & np.where(fwd, m > i, m < i)
    masks = [incl, strict, np.broadcast_to(fwd, (P, P)), np.broadcast_to(~fwd, (P, P))]

    def level(s):
        return strict & (m // (2 * s) == i // (2 * s)) & (m // s != i // s)
    masks += [level(1), level(1).T] + [level(s).T for s in (2, 4, 8, 16, 32)]
    small = [np.eye(P), incl, strict]
    masks += [np.concatenate([x[:CHUNK, :CHUNK], x[CHUNK:, CHUNK:]], 0) for x in small]
    t = np.arange(SEQ)
    c = np.arange(P)
    pc = 2 * np.pi * np.outer(c, c) / P
    pt = 2 * np.pi * (np.outer(t, t) % SEQ) / SEQ
    scale = 1.0 / np.sqrt(SEQ * P)
    cos_t = (np.cos(pt) * scale).reshape(2, P, SEQ).transpose(1, 0, 2).reshape(P, 2 * SEQ)
    sin_t = (-np.sin(pt) * scale).reshape(2, P, SEQ).transpose(1, 0, 2).reshape(P, 2 * SEQ)
    c2 = np.concatenate([x.astype(np.float64) for x in masks] + [np.cos(pc), np.sin(pc), cos_t, sin_t], 1)
    return c1, c2.astype(np.float32)


def build_layer(nc, x, c, ctx, c_ctx, w_mod, b_mod, g_pre, g_post, w1_gate, w1_up, w1_down, w_in, conv_w,
                a_log, dt_bias, g_onorm, w_out, w2_gate, w2_up, w2_down, const1, const2, out):
    with ExitStack() as es:
        R_XN = 16512
        R_ACC = R_XN + 65536
        R_H = R_ACC + 32768
        R_RAW = R_H + 16384
        R_PARTS = R_RAW + 32768
        R_TMP = R_PARTS + 32768
        R_QZ = R_TMP + 8192
        R_C = R_QZ + 16384
        R_END = 229344

        def sb(name, shape, offset, dt=F32):
            size = int(np.prod(shape[1:])) * 4
            assert offset % 32 == 0 and offset + size <= R_END, name
            return nc.alloc_sbuf_tensor_at(name, shape, dt, offset=offset)

        class Bump:
            def __init__(self, at, end):
                self.at, self.end = at, end

            def __call__(self, name, shape, dt=F32):
                t = sb(name, shape, self.at, dt)
                self.at += (int(np.prod(shape[1:])) * 4 + 31) // 32 * 32
                assert self.at <= self.end, name
                return t

        raw = sb("raw", [P, RAW_SLOTS, 2 * UNIT], R_RAW)
        parts = sb("parts", [P, PART_SLOTS, 2, UNIT], R_PARTS, F32R)
        xn = sb("xn", [P, 2, KT, TOK], R_XN, F32R)
        xn2 = sb("xn2", [P, 2, KT, SEQ], R_XN, F32R)
        x_in = sb("x_in", [P, 4, D], R_ACC)
        x_again = sb("x_again", [P, 4, D], R_XN)
        acc = sb("acc", [P, KT, TOK], R_ACC)
        acc2 = sb("acc2", [P, KT, SEQ], R_ACC)
        h_parts = sb("h_parts", [P, 2, GT, TOK], R_H, F32R)
        h2_parts = sb("h2_parts", [P, 2, GT, SEQ], R_H, F32R)
        x1 = sb("x1", [P, KT, SEQ], R_H)
        x2 = sb("x2", [P, KT, SEQ], R_XN + 32768)
        kv = sb("kv", [P, 2 * HEADS, TOK], R_ACC)
        qzf = sb("qzf", [P, 3 * HEADS, SEQ], R_TMP)
        silu_g = sb("silu_g", [P, 2, TOK], R_TMP)
        h_f32 = sb("h_f32", [P, 2, TOK], R_TMP + 4096)
        tmp = Bump(R_TMP, R_QZ)
        v_buf = tmp("v_buf", [P, 2, TOK])
        sq_buf = tmp("sq_buf", [P, 2, TOK])
        qz = Bump(R_QZ, R_C)
        rb = qz("rb", [P, TOK])
        cpad = qz("cpad", [P, KT, 32])
        mod_row = qz("mod_row", [P, 512])
        vec_rows = qz("vec_rows", [KT, N_VEC, P])
        junk = sb("junk", [P, D], R_PARTS)
        out_rows = sb("out_rows", [P, 2, D], R_PARTS)
        cb = Bump(R_C, R_END)
        c1 = cb("c1", [P, 2 * P])
        modT = cb("modT", [P, N_MOD, 2, KT])
        vecT = cb("vecT", [P, N_VEC, KT])
        convT = cb("convT", [P, 3 * HEADS, TAPS])
        pre_a = cb("pre_a", [P, 2, KT])
        post_g = cb("post_g", [P, 2, KT])
        ssq = cb("ssq", [P, 4])
        rstd = cb("rstd", [P, 4])
        onorm = cb("onorm", [P, 1])
        alog = cb("alog", [32, 1])
        dtb = cb("dtb", [32, 1])
        ealog = cb("ealog", [32, 1])
        conv_rows = sb("conv_rows", [24, TAPS, P], R_H)
        strict_b = cb("strict_b", [P, STEPS, CHUNK])
        o_out = cb("o_out", [P, SEQ])
        qh = cb("qh", [P, P])
        ident, ones = c1[:, 0:P], c1[:, P:2 * P]

        ra = Bump(R_RAW, R_PARTS)
        c2 = ra("c2", [P, C2_COLS])
        sc_all = ra("sc_all", [P, N_SC, HEADS, STEPS])
        g_T = ra("g_T", [P, STEPS, P])
        g_S = ra("g_S", [P, STEPS, P])
        g_Y = ra("g_Y", [P, STEPS, P])
        g_C = ra("g_C", [P, STEPS, P])
        sq_o = ra("sq_o", [P, SEQ])
        r_o = ra("r_o", [P, SEQ])
        sc = ra("sc", [P, N_HSC, STEPS])
        sc_b = ra("sc_b", [P, N_HSC, STEPS])
        r_k = ra("r_k", [P, STEPS])
        r_2 = ra("r_2", [P, STEPS + LSTEPS])
        taps = ra("taps", [P, 3, TAPS])
        rp = Bump(R_PARTS, R_TMP)
        kc = rp("kc", [P, TOK])
        vc = rp("vc", [P, TOK])
        qc = rp("qc", [P, SEQ])
        kp = rp("kp", [P, STEPS, P])
        vp = rp("vp", [P, STEPS, P])
        qp = rp("qp", [P, LSTEPS, P])
        kbg = rp("kbg", [P, STEPS, P])
        kd = rp("kd", [P, STEPS, P])
        vb = rp("vb", [P, STEPS, P])
        n_mat = rp("n_mat", [P, STEPS, P])
        f_out = rp("f_out", [P, SEQ])
        rx = Bump(R_XN + 32768, R_ACC)
        n_T = rx("n_T", [P, STEPS, P])
        gm = rx("gm", [P, STEPS, CHUNK])
        d_mat = rx("d_mat", [P, STEPS, CHUNK])
        dT = rx("dT", [P, LSTEPS, CHUNK])
        pT = rx("pT", [P, LSTEPS, CHUNK])
        wT = rx("wT", [P, STEPS, P])
        vt = rx("vt", [P, STEPS, P])
        u_buf = rx("u_buf", [P, 2, P])
        st = rx("st", [P, 2, P])
        o_buf = rx("o_buf", [P, LSTEPS, P])
        f_in = rx("f_in", [P, SEQ])
        f_mid = rx("f_mid", [P, 2, 2 * P])
        kd_b = rx("kd_b", [P, STEPS, P])
        pT_b = rx("pT_b", [P, LSTEPS, CHUNK])
        qp_b = rx("qp_b", [P, LSTEPS, P])
        def flat_front(t, n):
            return t[:].rearrange("p a b -> p (a b)")[:, 0:n * CHUNK].rearrange("p (a b) -> p a b", b=CHUNK)

        mask = [c2[:, n * P:(n + 1) * P] for n in range(N_FULL)]
        INCL, STRICT, HALF_F, HALF_B, M1, M1T = mask[:6]
        LEVEL_T = mask[6:]
        pair_mask = [c2[:, N_FULL * P + n * CHUNK:N_FULL * P + (n + 1) * CHUNK] for n in range(N_PAIR)]
        PAIR_ID, P_INCL, P_STRICT = pair_mask
        diag = flat_front(n_T, STEPS + LSTEPS)
        n_raw = flat_front(g_Y, STEPS)
        C_DFT = N_FULL * P + N_PAIR * CHUNK
        dft_c = c2[:, C_DFT:C_DFT + 2 * P]
        dft_t = c2[:, C_DFT + 2 * P:].rearrange("p (f t n) -> p f t n", f=2, t=2)
        HALVES = (slice(0, CHUNK), slice(CHUNK, P))

        def flat(ap):
            return ap.rearrange("p a b -> p (a b)")

        def grp(ap, g):
            return ap[:, 4 * g:4 * g + 4, :]

        def both(m):
            return m.unsqueeze(1).to_broadcast([P, 4, m.shape[1]])

        ps = es.enter_context(nc.psum_tensor("ps", [P, 8, 512], F32))

        def sem(name):
            return es.enter_context(nc.semaphore(name))

        vec_in, c1_in, x_re, c2_in, out_sem = sem("vec_in"), sem("c1_in"), sem("x_re"), sem("c2_in"), sem("out_sem")
        x_landed = [sem(f"x_landed{n}") for n in range(4)]
        raw_landed = [sem(f"raw_landed{n}") for n in range(RAW_SLOTS)]
        raw_free = [sem(f"raw_free{n}") for n in range(RAW_SLOTS)]
        hi_ready = sem("hi_ready")
        even_ready = sem("even_ready")
        units_done = sem("units_done")

        vecs_T, vecs_ok, c_ok, mod_T, mod_ok, mod_copied = (
            sem("vecs_T"), sem("vecs_ok"), sem("c_ok"), sem("mod_T"), sem("mod_ok"), sem("mod_copied"))
        cpad_zero = sem("cpad_zero")
        ssq_ok, ms_ok, root_ok, rb_ok, x_scaled, xT_ok, xT_used = (
            sem("ssq_ok"), sem("ms_ok"), sem("root_ok"), sem("rb_ok"), sem("x_scaled"), sem("xT_ok"), sem("xT_used"))
        v_ok, v_hi, xn_ok = sem("v_ok"), sem("v_hi"), sem("xn_ok")
        sq_ok, sq_used, gated, x_ok, scaled, consts_ok = (
            sem("sq_ok"), sem("sq_used"), sem("gated"), sem("x_ok"), sem("scaled"), sem("consts_ok"))
        kept = sem("kept")
        silu_ok, h_ok, h_hi, h_split, down_tile, down_added = (
            sem("silu_ok"), sem("h_ok"), sem("h_hi"), sem("h_split"), sem("down_tile"), sem("down_added"))
        in_copied = sem("in_copied")

        def chunk_src(w, rows, r0, n_rows, col, n_cols):
            return w[0].rearrange("(k p) n -> p k n", p=P)[:, ds(r0, n_rows), ds(col, n_cols)]

        mod_half, scaled_ctx = sem("mod_half"), sem("scaled_ctx")

        PER = {
            "taps_ok": 1, "center": 3, "conv": 20,
            "sc_ok": 1, "gm_ok": 2, "kp_ok": 2, "vp_ok": 2, "qp_ok": 2, "qq_mm": 1, "diag_ok": 2, "ss_ok": 1, "ss_eps": 1,
            "ss_inv": 1, "ss_root": 2, "coef_r2": 1, "coef_r": 2, "sb_ok": 2, "kvT": 4, "kbg_ok": 2, "kd_ok": 2,
            "vb_ok": 2, "e_mm": 2, "e_exp": 2, "kk_mm": 1, "qk_mm": 1, "n_half": 1, "n_ok": 2, "p_half": 1,
            "p_ok": 1, "nT_mm": 2, "nT_ok": 2, "ts_half": 4, "t_ok": 10, "s_ok": 12, "c_mask": 10, "y_mm": 10,
            "y_ok": 10, "x_mm": 10, "w_mm": 2, "vt_mm": 2, "w_ok": 2, "vt_ok": 2,
            "f_stage": 1, "f_a": 1, "f_mid_ok": 1, "f_b": 1, "f_v": 1, "f_hi": 1, "f_lo": 1,
            "b_sc": 1, "b_qp": 1, "b_kd": 1, "b_pT": 1, "st_zero": 1, "wh_mm": 8, "u_ok": 8, "dh_mm": 7,
            "st_ok": 14, "qh_mm": 4, "pu_mm": 4, "qh_ok": 4, "o_ok": 4, "oT_mm": 1, "osq": 1, "oss_mm": 1,
            "oss_eps": 1, "oss_root": 1, "oss_inv": 1, "z_ok": 1, "o_n1": 1, "o_n2": 1, "o_hi": 1, "o_lo": 1,
        }
        hs = {k: sem(k) for k in PER}
        out_copied, out_T = sem("out_copied"), sem("out_T")
        ab_sem = {k: sem(k) for k in ("ab_mm", "ab_x", "ab_abs", "ab_e", "ab_ln", "ab_w", "ab_wi", "ab_d", "ab_c",
                                      "ab_l", "ab_r", "ab_sp", "ab_g", "ab_b", "ab_ea", "abT", "abT_ok", "gcum",
                                      "gexp", "ab_bg", "ab_zero")}

        class Head:

            def __init__(self, eng, h):
                self.eng, self.h = eng, h

            def wait(self, name, n=None):
                self.eng.wait_ge(hs[name], self.h * PER[name] + (PER[name] if n is None else n))

            def last(self, *names):
                if isinstance(self.h, int) and self.h == 0:
                    return
                for name in names:
                    self.eng.wait_ge(hs[name], self.h * PER[name])

        def run_heads(eng, step):
            step(None, None, 0)
            step(0, None, 1)
            with eng.Fori(0, HEADS - 2) as i:
                step(i + 1, i, i + 2)
            step(HEADS - 1, HEADS - 2, None)
            step(None, HEADS - 1, None)

        tb = Bump(R_RAW + 4 * (C2_COLS + N_SC * HEADS * STEPS), R_PARTS)
        ab_x, ab_abs, ab_e, ab_ln, ab_w, ab_r, ab_b, ab_g = (tb(n, [32, TOK]) for n in (
            "ab_x", "ab_abs", "ab_e", "ab_ln", "ab_w", "ab_r", "ab_b", "ab_g"))
        ab_pair = sb("ab_pair", [32, 2, STEPS, P], R_PARTS)

        block = es.enter_context(nc.Block())

        @block.sync
        def _(sp):
            def load(seg, i, n, src):
                p = seg.pos + n
                slot, lap = p % RAW_SLOTS, p // RAW_SLOTS
                per = len(seg.pattern) // RAW_SLOTS
                sp.wait_ge(raw_free[slot], per * i + lap + 1)
                k = src.shape[1] if len(src.shape) == 3 else 1
                dst = raw[:, slot, :].rearrange("p (k n) -> p k n", k=k)
                sp.dma_start(dst, src).then_inc(raw_landed[slot], 16)

            def load_mod(seg, i, n, row, k):
                load(seg, i, n, chunk_src(w_mod, D, k, 1, row * D, D))

            def load_round(seg, i, g, mod_row_idx, gate, up, down):
                src = []
                for half in range(2):
                    for w in (gate, up):
                        for kh in range(2):
                            src.append(chunk_src(w, D, 8 * kh, 8, g * GROUP + 256 * half, 256))
                for nb in range(4):
                    src.append(chunk_src(down, DFF, g * GT, GT, 512 * nb, 512))
                for j, n in enumerate(seg.at):
                    load(seg, i, n, src[j])
                    if j < 8 and seg.mods:
                        for e in range(2):
                            load_mod(seg, i, seg.mods[2 * j + e], mod_row_idx, 2 * j + e)

            def load_pairs(seg, i, w, col):
                for j in range(4):
                    load(seg, i, j, chunk_src(w, D, 8 * (j % 2), 8, col + i * 512 + 256 * (j // 2), 256))

            for t in range(4):
                src = (ctx if t < 2 else x)[0, (t % 2) * P:(t % 2 + 1) * P, :]
                sp.dma_start(x_in[:, t, :], src).then_inc(x_landed[t], 16)
            with sp.Fori(0, 2) as i:
                for k in range(KT):
                    load_mod(S_MOD, i, k, i, k)
            with sp.Fori(0, S_A.iters) as i:
                load_round(S_A, i, i, i + 2, w1_gate, w1_up, w1_down)
            with sp.Fori(0, S_B.iters) as i:
                load_round(S_B, i, i + A_ROUNDS, None, w1_gate, w1_up, w1_down)
            with sp.Fori(0, S_KV.iters) as i:
                load_pairs(S_KV, i, w_in, 1024)
            with sp.Fori(0, 2) as i:
                load_pairs(S_Q, i, w_in, 0)
            with sp.Fori(0, 2) as i:
                load_pairs(S_Z, i, w_in, 3072)
            with sp.Fori(0, 2) as i:
                load_pairs(S_F, i, w_in, 4096 + 4 * HEADS)
            load(S_AB, 0, 0, chunk_src(w_in, D, 0, KT, 4096, P))
            sp.wait_ge(units_done, PART_SLOTS + 2 * S_OUT.weight)
            sp.dma_start(c2[:], const2).then_inc(c2_in, 16)
            sp.wait_ge(hs["o_lo"], HEADS)
            with sp.Fori(0, S_OUT.iters) as i:
                load_pairs(S_OUT, i, w_out, 0)
            with sp.Fori(0, S_F2.iters) as i:
                load_round(S_F2, i, i, None, w2_gate, w2_up, w2_down)
            load_round(S_F2L, 0, ROUNDS - 1, None, w2_gate, w2_up, w2_down)
            for t in range(2):
                sp.wait_ge(out_copied, 4 * (t + 1))
                sp.dma_start(out[0, t * P:(t + 1) * P, :], out_rows[:, t, :]).then_inc(out_sem, 16)
            sp.wait_ge(out_sem, 32)

        @block.gpsimd
        def _(pool):
            for n in range(RAW_SLOTS):
                pool.sem_inc(raw_free[n], 1)
            pool.sem_inc(units_done, PART_SLOTS)
            pool.sem_inc(h_ok, 1)
            pool.sem_inc(down_added, 1)
            pool.sem_inc(in_copied, 2)
            pool.sem_inc(mod_ok, 1)
            pool.wait_ge(units_done, PART_SLOTS + 2 * S_KV.weight)
            for t in range(4):
                src = (ctx if t < 2 else x)[0, (t % 2) * P:(t % 2 + 1) * P, :]
                pool.dma_start(x_again[:, t, :], src).then_inc(x_re, 16)

            def step(ha, hb, hc):
                if ha is not None:
                    a = Head(pool, ha)
                    a.wait("coef_r2")
                    a.last("n_ok")
                    for g in range(2):
                        nc.gpsimd.tensor_tensor(grp(strict_b, g), both(P_STRICT),
                                                sc[:, K_BR2, 4 * g:4 * g + 4].unsqueeze(2)
                                                .to_broadcast([P, 4, CHUNK]), ALU.mult).then_inc(hs["sb_ok"], 1)
                    for lv in range(5):
                        for g in range(2):
                            a.wait("nT_ok", g + 1)
                            if lv:
                                a.wait("y_mm", 2 * (lv - 1) + g + 1)
                            else:
                                a.last("y_mm")
                            nc.gpsimd.tensor_tensor(grp(g_C, g), grp(n_T, g), both(LEVEL_T[lv]), ALU.mult)\
                                .then_inc(hs["c_mask"], 1)

            run_heads(pool, step)

        def mixer_act(act):
            A = ab_sem
            act.wait_ge(A["ab_x"], 1)
            nc.scalar.activation(ab_abs[:], ab_x[:], ACT.Abs).then_inc(A["ab_abs"], 1)
            act.wait_ge(A["ab_abs"], 1)
            nc.scalar.activation(ab_e[:], ab_abs[:], ACT.Exp, scale=-1.0).then_inc(A["ab_e"], 1)
            nc.scalar.activation(ealog[:], alog[:], ACT.Exp).then_inc(A["ab_ea"], 1)
            act.wait_ge(A["ab_w"], 1)
            nc.scalar.activation(ab_ln[:], ab_w[:], ACT.Ln).then_inc(A["ab_ln"], 1)
            nc.scalar.activation(ab_b[:], ps[0:32, 0, :], ACT.Sigmoid).then_inc(A["ab_b"], 1)
            act.wait_ge(A["gcum"], 1)
            nc.scalar.activation(sc_all[:, K_GAMMA:N_SC].rearrange("p k h s -> p (k h s)"),
                                 ps[:, 3, 0:256], ACT.Exp).then_inc(A["gexp"], 1)

            def center(c):
                c.wait("taps_ok")
                c.last("kp_ok", "vp_ok", "qp_ok")
                for n, (dst, src) in enumerate(((kc, kv[:, ds(c.h, 1), :]), (vc, kv[:, ds(c.h + HEADS, 1), :]),
                                                (qc, qzf[:, ds(c.h, 1), :]))):
                    tap = (1, 2, 0)[n]
                    nc.scalar.activation(dst[:], flat(src), ACT.Copy, scale=taps[:, tap, 2:3])\
                        .then_inc(hs["center"], 1)

            def silu_pairs(dst, src, name, d):
                if dst is qp:
                    o = dst[:].rearrange("p c (d j) -> p d c j", d=2)[:, d, :, :]
                    i_ = src[:].rearrange("p (c j) -> p c j", j=CHUNK)
                    i_ = i_[:, ::-1, :] if d else i_
                else:
                    o = dst[:].rearrange("p (g c) (d j) -> p g c d j", g=2, d=2)[:, :, :, d, :]
                    i_ = src[:].rearrange("p (g c j) -> p g c j", g=2, j=CHUNK)
                    i_ = i_[:, :, ::-1, :] if d else i_
                nc.scalar.activation(o, i_, ACT.Silu).then_inc(hs[name], 1)

            def silu_k(c):
                c.wait("conv", 8)
                c.last("kvT", "kk_mm", "qk_mm")
                silu_pairs(kp, kc, "kp_ok", 0)
                silu_pairs(kp, kc, "kp_ok", 1)

            def silu_vq(c):
                c.wait("conv", 20)
                c.last("b_qp", "qq_mm")
                silu_pairs(vp, vc, "vp_ok", 0)
                silu_pairs(vp, vc, "vp_ok", 1)
                silu_pairs(qp, qc, "qp_ok", 0)
                silu_pairs(qp, qc, "qp_ok", 1)
                zt = flat(qzf[:, ds(c.h + HEADS, 1), :])
                nc.scalar.activation(zt, zt, ACT.Silu).then_inc(hs["z_ok"], 1)
                c.last("f_a")
                nc.scalar.activation(f_in[:], flat(qzf[:, ds(c.h + 2 * HEADS, 1), :]), ACT.Copy)\
                    .then_inc(hs["f_stage"], 1)

            def keep_for_scan(a, b):
                if b:
                    for name in ("dh_mm", "qh_mm", "st_ok", "pu_mm", "o_ok"):
                        b.wait(name)
                a.wait("kd_ok")
                a.wait("qp_ok")
                nc.scalar.activation(flat(kd_b[:]), flat(kd[:]), ACT.Copy).then_inc(hs["b_kd"], 1)
                nc.scalar.activation(flat(qp_b[:]), flat(qp[:]), ACT.Copy).then_inc(hs["b_qp"], 1)
                a.wait("p_ok")
                nc.scalar.activation(flat(pT_b[:]), flat(pT[:]), ACT.Copy).then_inc(hs["b_pT"], 1)
                a.wait("sc_ok")
                a.wait("ss_root")
                a.wait("coef_r")
                if b:
                    b.wait("qh_ok")
                nc.scalar.activation(flat(sc_b[:]), flat(sc[:]), ACT.Copy).then_inc(hs["b_sc"], 1)

            def decays(a):
                a.wait("e_mm", 1)
                nc.scalar.activation(flat(d_mat[:]), ps[:, 3, :], ACT.Exp).then_inc(hs["e_exp"], 1)
                a.wait("e_mm", 2)
                nc.scalar.activation(flat(dT[:]), ps[:, 2, 0:SEQ], ACT.Exp).then_inc(hs["e_exp"], 1)

            def transposed(a):
                a.wait("f_v")
                nc.scalar.activation(flat(xn2[:, 0, ds(a.h + HEADS, 1), :]), f_out[:], ACT.Copy)\
                    .then_inc(hs["f_hi"], 1)
                for g in range(2):
                    a.wait("nT_mm", g + 1)
                    nc.scalar.activation(flat(grp(n_T, g)), ps[:, 3 - 2 * g, :], ACT.Copy)\
                        .then_inc(hs["nT_ok"], 1)

            def norms(a):
                a.wait("ss_inv")
                a.last("vb_ok")
                a.last("b_sc")
                nc.scalar.activation(r_k[:], r_2[:, 0:STEPS], ACT.Sqrt).then_inc(hs["ss_root"], 1)
                nc.scalar.activation(sc[:, K_QS, 4:8], r_2[:, STEPS:], ACT.Sqrt, scale=1.0 / P)\
                    .then_inc(hs["ss_root"], 1)

            def y_out(a, lv, g):
                a.wait("y_mm", 2 * lv + g + 1)
                if lv:
                    a.wait("x_mm", 2 * (lv - 1) + g + 1)
                nc.scalar.activation(flat(grp(g_Y, g)), ps[:, g, :], ACT.Copy).then_inc(hs["y_ok"], 1)

            def query_state(b, s):
                t = s - 4
                b.wait("qh_mm", t + 1)
                if t:
                    b.wait("o_ok", t)
                nc.scalar.activation(qh[:], ps[:, 7, P:2 * P], ACT.Copy, scale=sc_b[:, K_GQS, s:s + 1])\
                    .then_inc(hs["qh_ok"], 1)

            def wv_out(a):
                for g in range(2):
                    a.wait("w_mm", g + 1)
                    nc.scalar.activation(flat(grp(wT, g)), ps[:, 2 + g, :], ACT.Copy).then_inc(hs["w_ok"], 1)
                for g in range(2):
                    a.wait("vt_mm", g + 1)
                    nc.scalar.activation(flat(grp(vt, g)), ps[:, g, :], ACT.Copy).then_inc(hs["vt_ok"], 1)

            def step(ha, hb, hc):
                a, b, c = (None if h is None else Head(act, h) for h in (ha, hb, hc))
                if a:
                    norms(a)
                    a.wait("f_a")
                    a.last("f_b")
                    nc.scalar.activation(flat(f_mid[:]), ps[:, 1, :], ACT.Copy).then_inc(hs["f_mid_ok"], 1)
                    decays(a)
                    transposed(a)
                for lv in range(5):
                    for g in range(2):
                        if a:
                            y_out(a, lv, g)
                        if b and lv < 2:
                            query_state(b, 4 + 2 * lv + g)
                        if b and lv == 2 and g == 0:
                            b.wait("oT_mm")
                            nc.scalar.activation(sq_o[:], ps[:, 7, 256:512], ACT.Square).then_inc(hs["osq"], 1)
                    if lv == 0 and c:
                        center(c)
                    if lv == 3 and b:
                        b.wait("oss_eps")
                        nc.scalar.activation(r_o[:], r_o[:], ACT.Sqrt).then_inc(hs["oss_root"], 1)
                    if lv == 3 and a:
                        keep_for_scan(a, b)
                    if lv == 3 and c:
                        silu_k(c)
                    if lv == 4 and b:
                        b.wait("o_n2")
                        nc.scalar.activation(flat(xn2[:, 0, ds(b.h, 1), :]), o_out[:], ACT.Copy)\
                            .then_inc(hs["o_hi"], 1)
                    if lv == 4 and c:
                        silu_vq(c)
                if a:
                    if b:
                        b.wait("u_ok")
                        b.wait("wh_mm")
                    wv_out(a)

            run_heads(act, step)

        @block.scalar
        def _(act):
            def split_hi(seg, i, j, b):
                n = len(seg.pattern) if j == len(seg.at) else seg.at[j]
                p = seg.pos + n
                w = seg.weight + j
                slot, lap = p % RAW_SLOTS, p // RAW_SLOTS
                unit = 2 * w + b
                if b == 0:
                    act.wait_ge(raw_landed[slot], 16 * (lap + 1) + 16 * (len(seg.pattern) // RAW_SLOTS) * i)
                act.wait_ge(units_done, unit + 1 + 2 * len(seg.at) * i)
                nc.scalar.activation(parts[:, unit % PART_SLOTS, 0, :], raw[:, slot, b * UNIT:(b + 1) * UNIT],
                                     ACT.Copy).then_inc(hi_ready, 1)

            def ffn_round(seg, i, G, N, gpart, mods, last=False):
                ubase = PART_SLOTS + 2 * seg.weight + 24 * i
                for u in range(24):
                    if u in (8, 16):
                        s = u // 8 - 1
                        act.wait_ge(h_ok, 2 * G + s + 2)
                        nc.scalar.activation(gpart[:, 0, 2 * s:2 * s + 2, :], h_f32[:, :, 0:N],
                                             ACT.Copy).then_inc(h_hi, 1)
                    if not (last and u >= 22):
                        split_hi(seg, i, u // 2 + 1, u % 2)
                    if u in (4, 12):
                        s = u // 12
                        act.wait_ge(units_done, ubase + u)
                        act.wait_ge(h_ok, 2 * G + s + 1)
                        nc.scalar.activation(silu_g[:, :, 0:N], ps[:, 4 * s:4 * s + 2, 0:N],
                                             ACT.Silu).then_inc(silu_ok, 1)
                    if mods and u == 17:
                        copy_mod_row(seg, i, i + 2)

            def copy_mod_row(seg, i, row):
                p = seg.pos + seg.mods[-1]
                act.wait_ge(raw_free[p % RAW_SLOTS], p // RAW_SLOTS + 2 + (len(seg.pattern) // RAW_SLOTS) * i)
                act.wait_ge(mod_ok, row + 1)
                nc.scalar.activation(mod_row[:], ps[:, 7, :], ACT.Copy).then_inc(mod_copied, 1)

            def root(n, cols, buf):
                act.wait_ge(ms_ok, n)
                nc.scalar.activation(buf, buf, ACT.Sqrt).then_inc(root_ok, 1)

            act.dma_start(c1[:], const1).then_inc(c1_in, 16)
            act.dma_start(vec_rows[:, V_CCTX, :], c_ctx.rearrange("(k p) -> k p", p=P)).then_inc(vec_in, 16)
            act.dma_start(vec_rows[:, V_C, :], c[0].rearrange("(k p) -> k p", p=P)).then_inc(vec_in, 16)
            act.dma_start(vec_rows[:, V_BMOD:V_BMOD + N_MOD, :],
                          b_mod[0].rearrange("(v k p) -> k v p", p=P, k=KT)).then_inc(vec_in, 16)
            act.dma_start(vec_rows[:, V_GPRE:V_GPRE + 3, :],
                          g_pre[0].rearrange("v (k p) -> k v p", p=P)).then_inc(vec_in, 16)
            act.dma_start(vec_rows[:, V_GPOST:V_GPOST + 3, :],
                          g_post[0].rearrange("v (k p) -> k v p", p=P)).then_inc(vec_in, 16)
            act.dma_start(conv_rows[:], conv_w[0].rearrange("t (k p) -> k t p", p=P)).then_inc(vec_in, 16)
            act.dma_start(onorm[:], g_onorm[0].rearrange("(p o) -> p o", o=1)).then_inc(vec_in, 16)
            act.wait_ge(cpad_zero, 3)
            act.dma_start(alog[0:16, :], a_log[0].rearrange("d (h o) -> (d h) o", o=1)).then_inc(vec_in, 16)
            act.dma_start(dtb[0:16, :], dt_bias[0].rearrange("d (h o) -> (d h) o", o=1)).then_inc(vec_in, 16)
            act.wait_ge(vecs_ok, 2)
            for s in range(2):
                nc.scalar.activation(cpad[:, :, s], vecT[:, V_CCTX + s, :], ACT.Silu).then_inc(c_ok, 1)
            for t in range(4):
                act.wait_ge(x_landed[t], 16)
                if t:
                    act.wait_ge(ssq_ok, t)
                nc.scalar.activation(junk[:], x_in[:, t, :], ACT.Square, accum_out=ssq[:, t:t + 1])\
                    .then_inc(ssq_ok, 1)
            root(1, 4, rstd[:])
            act.wait_ge(rb_ok, 1)
            for t in range(4):
                nc.scalar.activation(x_in[:, t, :], x_in[:, t, :], ACT.Copy, scale=rstd[:, t:t + 1])\
                    .then_inc(x_scaled, 1)
            with act.Fori(0, 2) as i:
                copy_mod_row(S_MOD, i, i)
            for k in range(KT):
                act.wait_ge(v_ok, 2 * k + 2)
                nc.scalar.activation(xn[:, 0, k, :], v_buf[:, k % 2, :], ACT.Copy).then_inc(v_hi, 1)
            act.wait_ge(raw_landed[S_A.pos % RAW_SLOTS], 16 * (S_A.pos // RAW_SLOTS + 1))
            for b in range(2):
                nc.scalar.activation(parts[:, b, 0, :], raw[:, S_A.pos % RAW_SLOTS, b * UNIT:(b + 1) * UNIT],
                                     ACT.Copy).then_inc(hi_ready, 1)
            with act.Fori(0, S_A.iters) as i:
                ffn_round(S_A, i, i, TOK, h_parts, True)
            with act.Fori(0, S_B.iters) as i:
                ffn_round(S_B, i, i + A_ROUNDS, TOK, h_parts, False)

            def post(r, N, a, kept_x=None):
                base = 32 * r
                for k in range(KT):
                    if k == 0:
                        if r == 1:
                            act.wait_ge(in_copied, 2 + 28)
                        else:
                            act.wait_ge(down_added, 1 + 16 * ROUNDS * (1 + r // 2))
                    if base + k >= 2:
                        act.wait_ge(sq_used, base + k - 1)
                    nc.scalar.activation(sq_buf[:, k % 2, 0:N], a[:, k, :], ACT.Square).then_inc(sq_ok, 1)
                root(2 + 2 * r, N, rb[:, 0:N])

            def pre(r, N, a, dst, keep):
                base = 32 * r + KT
                s0 = 0 if N == TOK else 1
                for k in range(KT):
                    act.wait_ge(x_ok, KT * r + k + 1)
                    act.wait_ge(sq_used, base + k - 1)
                    nc.scalar.activation(sq_buf[:, k % 2, 0:N], a[:, k, :], ACT.Square).then_inc(sq_ok, 1)
                    nc.scalar.activation(keep[:, k, :], a[:, k, N - SEQ:N], ACT.Copy).then_inc(kept, 1)
                root(3 + 2 * r, N, rb[:, 0:N])
                row = 3 * (r + 1)
                for k in range(KT):
                    act.wait_ge(scaled, KT * r + k + 1)
                    if k >= 2:
                        act.wait_ge(xn_ok, KT * (r + 1) + k - 1)
                    for s in range(s0, 2):
                        c0 = (s - s0) * SEQ
                        nc.scalar.activation(v_buf[:, k % 2, c0:c0 + SEQ], a[:, k, c0:c0 + SEQ], ACT.Identity,
                                             bias=modT[:, row, s, k:k + 1]).then_inc(v_ok, 1)
                    act.wait_ge(v_ok, [32, 64][r] + (2 - s0) * (k + 1))
                    nc.scalar.activation(dst[:, 0, k, :], v_buf[:, k % 2, 0:N], ACT.Copy).then_inc(v_hi, 1)

            def in_pairs(seg, i, N, dst, tile, done):
                ubase = PART_SLOTS + 2 * seg.weight + 8 * i
                for u in range(8):
                    split_hi(seg, i, u // 2 + 1, u % 2)
                    if u % 4 == 3:
                        pr = u // 4
                        act.wait_ge(units_done, ubase + u + 1)
                        nc.scalar.activation(dst[:, ds(tile + 4 * i + 2 * pr, 2), :],
                                             ps[:, 2 * pr:2 * pr + 2, 0:N], ACT.Copy).then_inc(in_copied, 1)

            post(0, TOK, acc)
            pre(0, TOK, acc, xn, x1)
            with act.Fori(0, S_KV.iters) as i:
                in_pairs(S_KV, i, TOK, kv, 0, 0)
            act.wait_ge(xn_ok, 2 * KT)
            with act.Fori(0, 2) as i:
                in_pairs(S_Q, i, SEQ, qzf, 0, 8)
            with act.Fori(0, 2) as i:
                in_pairs(S_Z, i, SEQ, qzf, HEADS, 12)
            with act.Fori(0, 2) as i:
                in_pairs(S_F, i, SEQ, qzf, 2 * HEADS, 16)

            mixer_act(act)

            def split_first(seg):
                for b in range(2):
                    unit = 2 * seg.weight + b
                    act.wait_ge(raw_landed[seg.pos % RAW_SLOTS], 16 * (seg.pos // RAW_SLOTS + 1))
                    nc.scalar.activation(parts[:, unit % PART_SLOTS, 0, :],
                                         raw[:, seg.pos % RAW_SLOTS, b * UNIT:(b + 1) * UNIT],
                                         ACT.Copy).then_inc(hi_ready, 1)
            split_first(S_OUT)
            with act.Fori(0, S_OUT.iters) as i:
                in_pairs(S_OUT, i, SEQ, acc2, 0, 20)
            post(1, SEQ, acc2)
            pre(1, SEQ, acc2, xn2, x2)
            with act.Fori(0, S_F2.iters) as i:
                ffn_round(S_F2, i, i + ROUNDS, SEQ, h2_parts, False)
            ffn_round(S_F2L, 0, 2 * ROUNDS - 1, SEQ, h2_parts, False, last=True)
            post(2, SEQ, acc2)
            for t in range(2):
                for q in range(4):
                    n = 4 * t + q
                    act.wait_ge(out_T, n + 1)
                    nc.scalar.activation(out_rows[:, t, 512 * q:512 * q + 512], ps[:, n, :], ACT.Copy)\
                        .then_inc(out_copied, 1)

        def mixer_dve(dve, link):
            A = ab_sem
            dve.wait_ge(units_done, PART_SLOTS + 2 * S_OUT.weight)
            nc.vector.tensor_scalar(ab_x[:], ps[0:32, 0, :], dtb[:, 0:1], None, ALU.add).then_inc(A["ab_x"], 1)
            dve.wait_ge(A["ab_e"], 1)
            nc.vector.tensor_scalar(ab_w[:], ab_e[:], 1.0, None, ALU.add).then_inc(A["ab_w"], 1)
            dve.wait_ge(A["ab_w"], 1)
            link(nc.vector.scalar_tensor_tensor(ab_r[:], ab_w[:], -1.0, ab_e[:], ALU.add, ALU.subtract))
            link(nc.vector.reciprocal(ab_g[:], ab_w[:]))
            link(nc.vector.tensor_tensor(ab_r[:], ab_r[:], ab_g[:], ALU.mult))
            dve.wait_ge(A["ab_ln"], 1)
            link(nc.vector.tensor_tensor(ab_r[:], ab_ln[:], ab_r[:], ALU.subtract))
            link(nc.vector.scalar_tensor_tensor(ab_g[:], ab_x[:], 0.0, ab_r[:], ALU.max, ALU.add))
            dve.wait_ge(A["ab_ea"], 1)
            link(nc.vector.tensor_scalar(ab_g[:], ab_g[:], ealog[:, 0:1], -1.0, ALU.mult, ALU.mult))
            dve.wait_ge(A["ab_b"], 1)
            for n, src in enumerate((ab_g, ab_b)):
                d4 = ab_pair[:, n].rearrange("p (g c) (d j) -> p g c d j", g=2, d=2)
                s4 = src[:].rearrange("p (g c j) -> p g c j", g=2, j=CHUNK)
                for g in range(2):
                    nc.vector.tensor_copy(d4[:, g, :, 0, :], s4[:, g, :, :]).then_inc(A["ab_sp"], 1)
                    nc.vector.tensor_copy(d4[:, g, :, 1, :], s4[:, g, ::-1, :]).then_inc(A["ab_sp"], 1)
            dve.wait_ge(A["abT"], 1)
            for n in range(2):
                tr = ps[:, 1 + n, 0:256].rearrange("p (s a h) -> p a h s", a=4, h=HEADS)
                for half in range(2):
                    rows = slice(64 * half, 64 * half + 64)
                    nc.vector.tensor_copy(sc_all[rows, n, :, :], tr[rows, 2 * n + half, :, :])\
                        .then_inc(A["abT_ok"], 1)
            dve.wait_ge(A["gexp"], 1)
            dve.wait_ge(A["abT_ok"], 4)
            nc.vector.tensor_tensor(sc_all[:, K_BG].rearrange("p h s -> p (h s)"),
                                    sc_all[:, K_BETA].rearrange("p h s -> p (h s)"),
                                    sc_all[:, K_GAMMA].rearrange("p h s -> p (h s)"), ALU.mult)\
                .then_inc(A["ab_bg"], 1)
            dve.wait_ge(A["ab_bg"], 1)

            link(nc.vector.memset(n_mat[:], 0.0))
            link(nc.vector.memset(sc[:], 0.0))

            def coef(k, g, width):
                return sc[:, k, 4 * g:4 * g + 4].unsqueeze(2).to_broadcast([P, 4, width])

            def take_taps(c):
                c.last("conv", "center")
                nc.vector.tensor_copy(taps[:], convT[:].rearrange("p (q h) t -> p q h t", h=HEADS)
                                      [:, :, ds(c.h, 1), :].rearrange("p q h t -> p q (h t)")).then_inc(hs["taps_ok"], 1)

            def conv(c, n):
                t = min(n // 8, 2)
                spans = 2 if t < 2 else 1
                j = (0, 1, 3, 4)[(n - 8 * t) // spans]
                span = n % 2 if spans == 2 else 1
                dst, src, tap = ((kc, kv[:, ds(c.h, 1), :], 1), (vc, kv[:, ds(c.h + HEADS, 1), :], 2),
                                 (qc, qzf[:, ds(c.h, 1), :], 0))[t]
                src = flat(src)
                sh = j - 2
                if span == 0:
                    a, b = max(0, -sh), CTX - max(0, sh)
                    o, s_ = dst[:, a:b], src[:, a + sh:b + sh]
                else:
                    a, b = max(0, -sh), ROW - max(0, sh)
                    base = CTX if spans == 2 else 0
                    o = dst[:, base:base + SEQ].rearrange("p (r w) -> p r w", w=ROW)[:, :, a:b]
                    s_ = src[:, base:base + SEQ].rearrange("p (r w) -> p r w", w=ROW)[:, :, a + sh:b + sh]
                c.wait("center", t + 1)
                if n - 8 * t >= spans:
                    c.wait("conv", n - spans + 1)
                nc.vector.scalar_tensor_tensor(o, s_, taps[:, tap, j:j + 1], o, ALU.mult, ALU.add)\
                    .then_inc(hs["conv"], 1)

            def scalars(a):
                a.last("b_sc", "vb_ok", "kbg_ok", "kd_ok", "sb_ok", "gm_ok", "coef_r")
                nc.vector.tensor_copy(sc[:, 0:N_SC], sc_all[:, :, ds(a.h, 1), :].rearrange("p k h s -> p k (h s)"))\
                    .then_inc(hs["sc_ok"], 1)
                a.wait("sc_ok")
                a.last("e_mm")
                for g in range(2):
                    nc.vector.tensor_tensor(grp(gm, g), both(P_STRICT), coef(K_G, g, CHUNK), ALU.mult)\
                        .then_inc(hs["gm_ok"], 1)

            def norms(a):
                a.wait("kk_mm")
                a.wait("qq_mm")
                a.last("c_mask")
                for bank, n0, n in ((0, 0, STEPS), (1, STEPS, LSTEPS)):
                    nc.vector.tensor_tensor(diag[:, n0:n0 + n, :],
                                            ps[:, bank, 0:CHUNK * n].rearrange("p (s c) -> p s c", c=CHUNK),
                                            PAIR_ID.unsqueeze(1).to_broadcast([P, n, CHUNK]), ALU.mult)\
                        .then_inc(hs["diag_ok"], 1)
                a.wait("diag_ok")
                a.last("ss_root")
                nc.vector.tensor_reduce(r_2[:], diag, axis=mybir.AxisListType.X, op=ALU.add).then_inc(hs["ss_ok"], 1)
                a.wait("ss_ok")
                nc.vector.tensor_scalar(r_2[:], r_2[:], EPS, None, ALU.add).then_inc(hs["ss_eps"], 1)
                a.wait("ss_eps")
                nc.vector.reciprocal(r_2[:], r_2[:]).then_inc(hs["ss_inv"], 1)
                a.wait("ss_inv")
                nc.vector.tensor_tensor(sc[:, K_BR2:K_BR2 + 2, :], sc[:, K_BETA:K_BETA + 2, :],
                                        r_2[:, 0:STEPS].unsqueeze(1).to_broadcast([P, 2, STEPS]), ALU.mult)\
                    .then_inc(hs["coef_r2"], 1)
                a.wait("coef_r2")

            def token_k(a, g):
                a.last("b_kd", "w_mm")
                a.wait("kvT", g + 3)
                src = ps[:, 2 + g, :].rearrange("p (s c) -> p s c", s=4)
                nc.vector.tensor_tensor(grp(kd, g), src, coef(K_KD, g, P), ALU.mult).then_inc(hs["kd_ok"], 1)
                nc.vector.tensor_tensor(grp(kbg, g), src, coef(K_BGR2, g, P), ALU.mult).then_inc(hs["kbg_ok"], 1)

            def fnet_out(a):
                a.wait("f_b")
                a.last("f_lo")
                nc.vector.tensor_copy(f_out[:], ps[:, 1, 0:SEQ]).then_inc(hs["f_v"], 1)

            def chunk_half(a):
                a.wait("e_exp", 1)
                a.wait("kk_mm")
                a.last("x_mm")
                nc.vector.tensor_tensor(n_raw, d_mat[:], ps[:, 0, :].rearrange("p (s c) -> p s c", c=CHUNK),
                                        ALU.mult).then_inc(hs["n_half"], 1)

            def chunk_matrix(a):
                a.wait("sb_ok")
                a.wait("n_half")
                a.last("nT_mm", "ts_half")
                for rows in HALVES:
                    nc.vector.tensor_tensor(n_mat[rows, :, rows], n_raw[rows], strict_b[rows], ALU.mult)\
                        .then_inc(hs["n_ok"], 1)
                a.wait("n_ok")
                a.last("t_ok", "s_ok", "y_mm", "w_mm", "vt_mm")
                for g in range(2):
                    nc.vector.tensor_tensor(grp(g_T, g), grp(n_mat, g), both(M1), ALU.mult)\
                        .then_inc(hs["ts_half"], 1)

            def first_level(a):
                for g in range(2):
                    a.wait("ts_half", g + 1)
                    nc.vector.tensor_tensor(grp(g_T, g), both(ident), grp(g_T, g), ALU.subtract)\
                        .then_inc(hs["t_ok"], 1)
                for g in range(2):
                    a.wait("nT_ok", g + 1)
                    nc.vector.tensor_tensor(grp(g_S, g), grp(n_T, g), both(M1T), ALU.mult)\
                        .then_inc(hs["ts_half"], 1)
                for g in range(2):
                    a.wait("ts_half", g + 3)
                    nc.vector.tensor_tensor(grp(g_S, g), both(ident), grp(g_S, g), ALU.subtract)\
                        .then_inc(hs["s_ok"], 1)

            def late(a):
                a.wait("ss_root")
                nc.vector.tensor_tensor(sc[:, K_BR, :], sc[:, K_BETA, :], r_k[:], ALU.mult)\
                    .then_inc(hs["coef_r"], 1)
                nc.vector.tensor_tensor(sc[:, K_GQS, 4:8], sc[:, K_GAMMA, 4:8], sc[:, K_QS, 4:8], ALU.mult)\
                    .then_inc(hs["coef_r"], 1)
                a.wait("coef_r")
                for g in range(2):
                    a.wait("kvT", 1 + g)
                    src = ps[:, 4 + g, :].rearrange("p (s c) -> p s c", s=4)
                    nc.vector.tensor_tensor(grp(vb, g), src, coef(K_BR, g, P), ALU.mult).then_inc(hs["vb_ok"], 1)
                a.wait("e_exp", 2)
                a.wait("qk_mm")
                a.last("b_pT")
                nc.vector.tensor_tensor(flat(pT[:]), flat(dT[:]), ps[:, 2, SEQ:2 * SEQ], ALU.mult)\
                    .then_inc(hs["p_half"], 1)
                a.wait("p_half")
                nc.vector.tensor_tensor(pT[:], pT[:], both(P_INCL), ALU.mult).then_inc(hs["p_ok"], 1)
                a.wait("f_hi")
                row = flat(xn2[:, 0, ds(a.h + HEADS, 1), :]).bitcast(F32)
                nc.vector.tensor_tensor(flat(xn2[:, 1, ds(a.h + HEADS, 1), :]), f_out[:], row, ALU.subtract)\
                    .then_inc(hs["f_lo"], 1)

            def level(a, lv, g):
                a.wait("x_mm", 2 * lv + g + 1)
                if lv < 4:
                    a.wait("t_ok", 2 * lv + g + 1)
                    nc.vector.tensor_tensor(grp(g_T, g), grp(g_T, g),
                                            ps[:, 2 + g, :].rearrange("p (s c) -> p s c", s=4),
                                            ALU.subtract).then_inc(hs["t_ok"], 1)
                a.wait("s_ok", 2 * lv + g + 1)
                nc.vector.tensor_tensor(grp(g_S, g), grp(g_S, g),
                                        ps[:, 4 + g, :].rearrange("p (s c) -> p s c", s=4),
                                        ALU.subtract).then_inc(hs["s_ok"], 1)

            def scan_u(b, s):
                b.wait("vt_ok")
                b.wait("wh_mm", s + 1)
                if s >= 2:
                    b.wait("dh_mm", s - 1)
                if s >= 6:
                    b.wait("pu_mm", s - 5)
                nc.vector.tensor_tensor(u_buf[:, s % 2, :], vt[:, s, :], ps[:, 6, 256:256 + P], ALU.subtract)\
                    .then_inc(hs["u_ok"], 1)

            def scan_state(b, s):
                if s < STEPS - 1:
                    b.wait("dh_mm", s + 1)
                    b.wait("wh_mm", s + 1)
                    if s >= 4:
                        b.wait("qh_mm", s - 3)
                    if s:
                        b.wait("st_ok", 2 * s)
                    for d in range(2):
                        if d and s >= 4:
                            b.wait("pu_mm", s - 3)
                        nc.vector.scalar_tensor_tensor(st[:, d, :], st[:, d, :],
                                                       sc_b[:, K_LASTF + d, s:s + 1], ps[:, 6 + d, 0:P],
                                                       ALU.mult, ALU.add).then_inc(hs["st_ok"], 1)
                if s >= 4:
                    t = s - 4
                    b.wait("qh_ok", t + 1)
                    b.wait("pu_mm", t + 1)
                    nc.vector.scalar_tensor_tensor(o_buf[:, t, :], ps[:, 7, 2 * P:3 * P], sc_b[:, K_QS, s:s + 1],
                                                   qh[:], ALU.mult, ALU.add).then_inc(hs["o_ok"], 1)

            def scan_start(b):
                b.wait("b_sc")
                b.last("wh_mm", "qh_mm", "oT_mm", "st_ok", "pu_mm")
                nc.vector.memset(st[:], 0.0).then_inc(hs["st_zero"], 1)
                b.wait("st_zero")

            def output(b, part):
                if part == 0:
                    b.wait("oss_mm")
                    nc.vector.tensor_scalar(r_o[:], ps[:, 6, 0:SEQ], 1.0 / P, EPS, ALU.mult, ALU.add)\
                        .then_inc(hs["oss_eps"], 1)
                    return
                b.wait("oss_root")
                nc.vector.reciprocal(r_o[:], r_o[:]).then_inc(hs["oss_inv"], 1)
                b.wait("oss_inv")
                b.last("o_hi", "o_lo")
                nc.vector.scalar_tensor_tensor(o_out[:], ps[:, 7, 256:512], onorm[:, 0:1], r_o[:],
                                               ALU.mult, ALU.mult).then_inc(hs["o_n1"], 1)
                b.wait("o_n1")
                b.wait("z_ok")
                nc.vector.tensor_tensor(o_out[:], o_out[:], flat(qzf[:, ds(b.h + HEADS, 1), :]), ALU.mult)\
                    .then_inc(hs["o_n2"], 1)

            def output_lo(b):
                b.wait("o_hi")
                nc.vector.tensor_tensor(flat(xn2[:, 1, ds(b.h, 1), :]), o_out[:],
                                        flat(xn2[:, 0, ds(b.h, 1), :]).bitcast(F32), ALU.subtract)\
                    .then_inc(hs["o_lo"], 1)

            def step(ha, hb, hc):
                a, b, c = (None if h is None else Head(dve, h) for h in (ha, hb, hc))
                if a:
                    scalars(a)
                if c:
                    take_taps(c)
                if b:
                    scan_start(b)
                if a:
                    norms(a)
                if b:
                    scan_u(b, 0)
                if a:
                    token_k(a, 0)
                if b:
                    scan_state(b, 0)
                if a:
                    token_k(a, 1)
                if b:
                    scan_u(b, 1)
                    scan_state(b, 1)
                if a:
                    fnet_out(a)
                if b:
                    scan_u(b, 2)
                    scan_state(b, 2)
                if a:
                    chunk_half(a)
                if b:
                    scan_u(b, 3)
                if a:
                    chunk_matrix(a)
                if b:
                    scan_state(b, 3)
                if a:
                    late(a)
                    first_level(a)
                for lv in range(5):
                    for g in range(2):
                        if b and lv < 2:
                            scan_u(b, 4 + 2 * lv + g)
                            if g == 0:
                                scan_state(b, 4 + 2 * lv)
                        if b and lv == 3 and g == 0:
                            output(b, 0)
                        if a:
                            level(a, lv, g)
                        if b and lv < 2 and g == 1:
                            scan_state(b, 5 + 2 * lv)
                    if c and lv < 3:
                        for n in range((0, 6, 12)[lv], (6, 12, 20)[lv]):
                            conv(c, n)
                    if b and lv == 3:
                        output(b, 1)
                    if b and lv == 4:
                        output_lo(b)

            run_heads(dve, step)

        @block.vector
        def _(dve):
            own = sem("dve_own")
            own_n = [0]

            def link(ins):
                ins.then_inc(own, 1)
                own_n[0] += 1
                dve.wait_ge(own, own_n[0])

            def split_lo(seg, i, j, b):
                n = len(seg.pattern) if j == len(seg.at) else seg.at[j]
                p = seg.pos + n
                w = seg.weight + j
                slot = p % RAW_SLOTS
                unit = 2 * w + b
                pslot = unit % PART_SLOTS
                dve.wait_ge(hi_ready, unit + 1 + 2 * len(seg.at) * i)
                nc.vector.tensor_tensor(parts[:, pslot, 1, :], raw[:, slot, b * UNIT:(b + 1) * UNIT],
                                        parts[:, pslot, 0, :].bitcast(F32), ALU.subtract)\
                    .then_inc(raw_free[slot] if b else even_ready, 1)

            def split_first(seg):
                for b in range(2):
                    split_lo(seg, 0, 0, b)

            def ffn_round(seg, i, G, N, gpart, a, mods, last=False):
                ubase = PART_SLOTS + 2 * seg.weight + 24 * i
                for u in range(24):
                    if u in (8, 16):
                        s = u // 8 - 1
                        dve.wait_ge(units_done, ubase + u)
                        dve.wait_ge(silu_ok, 2 * G + s + 1)
                        up = 2 if s == 0 else 0
                        nc.vector.tensor_tensor(h_f32[:, :, 0:N], silu_g[:, :, 0:N], ps[:, up:up + 2, 0:N],
                                                ALU.mult).then_inc(h_ok, 1)
                        dve.wait_ge(h_hi, 2 * G + s + 1)
                        nc.vector.tensor_tensor(gpart[:, 1, 2 * s:2 * s + 2, :], h_f32[:, :, 0:N],
                                                gpart[:, 0, 2 * s:2 * s + 2, :].bitcast(F32), ALU.subtract)\
                            .then_inc(h_split, 1)
                    if not (last and u >= 22):
                        split_lo(seg, i, u // 2 + 1, u % 2)
                    if u >= 16 and u % 2:
                        j = (u - 17) // 2
                        for t in range(4):
                            bank = (2, 3, 6, 4)[t]
                            if t < 3:
                                dve.wait_ge(down_tile, 12 * G + 3 * j + t + 1)
                            else:
                                dve.wait_ge(units_done, ubase + u + 1)
                            nc.vector.tensor_tensor(a[:, 4 * j + t, :], a[:, 4 * j + t, :], ps[:, bank, 0:N],
                                                    ALU.add).then_inc(down_added, 1)
                    if mods and u == 19:
                        place_mod(i + 2)

            def place_mod(row):
                dve.wait_ge(mod_T, row + 1)
                src = ps[:, 5, :].rearrange("p (j c t) -> p t c j", c=4, t=32)
                for s in range(2):
                    ins = nc.vector.tensor_tensor(
                        modT[:, ds(row, 1), s, :].rearrange("p a (c j) -> p (a c) j", c=4), src[:, s, :, :],
                        vecT[:, ds(row + V_BMOD, 1), :].rearrange("p a (c j) -> p (a c) j", c=4), ALU.add)
                    ins.then_inc(mod_ok if s else mod_half, 1)

            nc.vector.memset(cpad[:], 0.0).then_inc(cpad_zero, 1)
            nc.vector.memset(alog[:], 0.0).then_inc(cpad_zero, 1)
            nc.vector.memset(dtb[:], 0.0).then_inc(cpad_zero, 1)
            dve.wait_ge(cpad_zero, 3)
            dve.wait_ge(vecs_T, 1)
            nc.vector.tensor_copy(vecT[:].rearrange("p a b -> p (a b)"), ps[:, 6, 0:N_VEC * KT]).then_inc(vecs_ok, 1)
            nc.vector.tensor_copy(convT[:].rearrange("p k t -> p t k"),
                                  ps[:, 6, N_VEC * KT:N_VEC * KT + 3 * HEADS * TAPS]
                                  .rearrange("p (t k) -> p t k", t=TAPS)).then_inc(vecs_ok, 1)
            dve.wait_ge(ssq_ok, 4)
            nc.vector.tensor_scalar(rstd[:], ssq[:], 1.0 / D, EPS, ALU.mult, ALU.add).then_inc(ms_ok, 1)
            dve.wait_ge(root_ok, 1)
            nc.vector.reciprocal(rstd[:], rstd[:]).then_inc(rb_ok, 1)
            with dve.Fori(0, 2) as i:
                place_mod(i)

            def pre_scalars(r):
                for s in range(2):
                    link(nc.vector.scalar_tensor_tensor(pre_a[:, s, :], modT[:, 3 * r + 1, s, :], 1.0,
                                                        vecT[:, V_GPRE + r, :], ALU.add, ALU.mult))

            def post_scalars(r, w):
                for s in range(2):
                    link(nc.vector.scalar_tensor_tensor(post_g[:, s, :], modT[:, 3 * r + 2, s, :], w,
                                                        vecT[:, V_GPOST + r, :], ALU.mult, ALU.mult))

            dve.wait_ge(mod_ok, 3)
            pre_scalars(0)
            for k in range(KT):
                dve.wait_ge(xT_ok, k + 1)
                if k >= 2:
                    dve.wait_ge(v_hi, k - 1)
                    dve.wait_ge(xn_ok, k - 1)
                for s in range(2):
                    nc.vector.tensor_scalar(v_buf[:, k % 2, s * CTX:(s + 1) * CTX],
                                            ps[:, k % 4, s * CTX:(s + 1) * CTX],
                                            pre_a[:, s, k:k + 1], modT[:, 0, s, k:k + 1],
                                            ALU.mult, ALU.add).then_inc(v_ok, 1)
                dve.wait_ge(v_hi, k + 1)
                nc.vector.tensor_tensor(xn[:, 1, k, :], v_buf[:, k % 2, :], xn[:, 0, k, :].bitcast(F32),
                                        ALU.subtract).then_inc(xn_ok, 1)
            split_first(S_A)
            dve.wait_ge(xT_ok, KT)
            dve.wait_ge(v_ok, 2 * KT)
            link(nc.vector.memset(acc[:], 0.0))
            with dve.Fori(0, S_A.iters) as i:
                ffn_round(S_A, i, i, TOK, h_parts, acc, True)
            with dve.Fori(0, S_B.iters) as i:
                ffn_round(S_B, i, i + A_ROUNDS, TOK, h_parts, acc, False)

            def inv_root(n, src, N, total):
                dve.wait_ge(sq_used, total)
                nc.vector.tensor_scalar(rb[:, 0:N], src, 1.0 / D, EPS, ALU.mult, ALU.add).then_inc(ms_ok, 1)
                dve.wait_ge(root_ok, n)
                nc.vector.reciprocal(rb[:, 0:N], rb[:, 0:N]).then_inc(rb_ok, 1)
                dve.wait_ge(rb_ok, n)

            def post(r, N, w, a, resid):
                post_scalars(r, w)
                s0 = 0 if N == TOK else 1
                inv_root(2 + 2 * r, ps[:, 7, 0:N], N, 32 * r + KT)
                for k in range(KT):
                    for s in range(s0, 2):
                        c0 = (s - s0) * SEQ
                        nc.vector.scalar_tensor_tensor(a[:, k, c0:c0 + SEQ], a[:, k, c0:c0 + SEQ],
                                                       post_g[:, s, k:k + 1], rb[:, c0:c0 + SEQ],
                                                       ALU.mult, ALU.mult).then_inc(gated, 1)
                    dve.wait_ge(gated, [0, 32, 48][r] + (2 - s0) * (k + 1))
                    if resid is None:
                        dve.wait_ge(xT_ok, KT + k + 1)
                        src = ps[:, k % 4, :]
                    else:
                        src = resid[:, k, :]
                    nc.vector.tensor_tensor(a[:, k, :], a[:, k, :], src, ALU.add).then_inc(x_ok, 1)

            def pre(r, N, a, dst):
                pre_scalars(r + 1)
                s0 = 0 if N == TOK else 1
                inv_root(3 + 2 * r, ps[:, 7, 0:N], N, 32 * (r + 1))

                def lo(k):
                    dve.wait_ge(v_hi, KT * (r + 1) + k + 1)
                    nc.vector.tensor_tensor(dst[:, 1, k, :], v_buf[:, k % 2, 0:N], dst[:, 0, k, :].bitcast(F32),
                                            ALU.subtract).then_inc(xn_ok, 1)
                dve.wait_ge(kept, KT * (r + 1))
                for k in range(KT):
                    for s in range(s0, 2):
                        c0 = (s - s0) * SEQ
                        ins = nc.vector.scalar_tensor_tensor(a[:, k, c0:c0 + SEQ], a[:, k, c0:c0 + SEQ],
                                                             pre_a[:, s, k:k + 1], rb[:, c0:c0 + SEQ],
                                                             ALU.mult, ALU.mult)
                        ins.then_inc(scaled if s else scaled_ctx, 1)
                    if k:
                        lo(k - 1)
                lo(KT - 1)

            post(0, TOK, 0.5, acc, None)
            pre(0, TOK, acc, xn)

            def in_split(seg, i):
                for u in range(8):
                    split_lo(seg, i, u // 2 + 1, u % 2)

            with dve.Fori(0, S_KV.iters) as i:
                in_split(S_KV, i)
            for seg in (S_Q, S_Z, S_F):
                with dve.Fori(0, 2) as i:
                    in_split(seg, i)

            mixer_dve(dve, link)

            split_first(S_OUT)
            with dve.Fori(0, S_OUT.iters) as i:
                in_split(S_OUT, i)
            post(1, SEQ, 1.0, acc2, x1)
            pre(1, SEQ, acc2, xn2)
            link(nc.vector.memset(acc2[:], 0.0))
            with dve.Fori(0, S_F2.iters) as i:
                ffn_round(S_F2, i, i + ROUNDS, SEQ, h2_parts, acc2, False)
            ffn_round(S_F2L, 0, 2 * ROUNDS - 1, SEQ, h2_parts, acc2, False, last=True)
            post(2, SEQ, 0.5, acc2, x2)

        def mixer_pe(pe):
            A = ab_sem

            def mm(o, lhsT, rhs, start=True, stop=True):
                return nc.tensor.matmul(o, lhsT, rhs, start=start, stop=stop)

            pe.wait_ge(A["ab_sp"], 8)
            for n in range(2):
                for s in range(STEPS):
                    last = nc.tensor.transpose(ps[:, 1 + n, 32 * s:32 * s + 32], ab_pair[:, n, s, :], c1[0:32, 0:32])
            last.then_inc(A["abT"], 1)
            pe.wait_ge(A["abT_ok"], 4)
            pe.wait_ge(c2_in, 16)
            g_all = sc_all[:, K_G].rearrange("p h s -> p (h s)")
            for n, m_ in enumerate((INCL, STRICT, HALF_F, HALF_B)):
                last = mm(ps[:, 3, 64 * n:64 * n + 64], m_, g_all)
            last.then_inc(A["gcum"], 1)
            pe.wait_ge(A["gexp"], 1)

            def inc(ins, name):
                ins.then_inc(hs[name], 1)

            def pair_mm(bank, col, lhsT, rhs, width=CHUNK):
                for rows in HALVES:
                    last = mm(ps[rows, bank, col:col + width], lhsT[rows], rhs[rows])
                return last

            def token_v(a):
                a.wait("vp_ok")
                a.last("s_ok")
                for g in range(2):
                    for s in range(4):
                        last = nc.tensor.transpose(ps[:, 4 + g, P * s:P * s + P], vp[:, 4 * g + s, :], ident)
                    inc(last, "kvT")

            def token_k(a):
                a.wait("kp_ok")
                a.last("w_ok")
                for g in range(2):
                    for s in range(4):
                        last = nc.tensor.transpose(ps[:, 2 + g, P * s:P * s + P], kp[:, 4 * g + s, :], ident)
                    inc(last, "kvT")

            def products_k(a):
                a.wait("kp_ok")
                a.last("vt_ok")
                for s in range(STEPS):
                    for rows in HALVES:
                        last = mm(ps[rows, 0, CHUNK * s:CHUNK * s + CHUNK], kp[:, s, rows], kp[:, s, rows])
                inc(last, "kk_mm")
                a.wait("qp_ok")
                for s in range(LSTEPS):
                    for rows in HALVES:
                        last = mm(ps[rows, 1, CHUNK * s:CHUNK * s + CHUNK], qp[:, s, rows], qp[:, s, rows])
                inc(last, "qq_mm")

            def fnet_channels(a):
                a.wait("f_stage")
                a.wait("diag_ok")
                for t in range(2):
                    last = mm(ps[:, 1, 256 * t:256 * t + 256], f_in[:, P * t:P * t + P], dft_c)
                inc(last, "f_a")

            def fnet_positions(a):
                a.wait("f_mid_ok")
                for n, (f, t) in enumerate(((0, 0), (0, 1), (1, 0), (1, 1))):
                    last = mm(ps[:, 1, 0:SEQ], f_mid[:, t, P * f:P * f + P], dft_t[:, f, t, :], n == 0, n == 3)
                inc(last, "f_b")

            def decay_sums(a):
                a.wait("gm_ok")
                a.wait("kd_ok")
                a.wait("kbg_ok")
                inc(mm(ps[:, 3, :], INCL, flat(gm[:])), "e_mm")

            def products_q(a):
                a.wait("qp_ok")
                for s in range(LSTEPS):
                    for rows in HALVES:
                        last = mm(ps[rows, 2, SEQ + CHUNK * s:SEQ + CHUNK * s + CHUNK], kp[:, 4 + s, rows],
                                  qp[:, s, rows])
                inc(last, "qk_mm")
                for s in range(LSTEPS):
                    last = pair_mm(2, CHUNK * s, gm[:, 4 + s, :], P_INCL)
                inc(last, "e_mm")

            def transposed(a):
                a.wait("e_exp", 1)
                a.wait("f_v")
                a.wait("n_ok")
                for g in range(2):
                    for s in range(4):
                        last = mm(ps[:, 3 - 2 * g, P * s:P * s + P], n_mat[:, 4 * g + s, :], ident)
                    inc(last, "nT_mm")

            def y_level(a, lv, g):
                a.wait("t_ok", 2 * lv + g + 1)
                a.wait("c_mask", 2 * lv + g + 1)
                if lv:
                    a.wait("y_ok", 2 * (lv - 1) + g + 1)
                else:
                    a.wait("n_half")
                    a.wait("nT_ok")
                for s in range(4 * g, 4 * g + 4):
                    last = mm(ps[:, g, P * (s % 4):P * (s % 4) + P], g_C[:, s, :], g_T[:, s, :])
                inc(last, "y_mm")

            def x_level(a, lv, g):
                a.wait("y_ok", 2 * lv + g + 1)
                a.wait("s_ok", 2 * lv + g + 1)
                if lv == 0:
                    a.wait("vb_ok", g + 1)
                    a.wait("p_half")
                    a.wait("nT_ok")
                if lv < 4:
                    for s in range(4 * g, 4 * g + 4):
                        mm(ps[:, 2 + g, P * (s % 4):P * (s % 4) + P], g_S[:, s, :], g_Y[:, s, :])
                for s in range(4 * g, 4 * g + 4):
                    last = mm(ps[:, 4 + g, P * (s % 4):P * (s % 4) + P], g_Y[:, s, :], g_S[:, s, :])
                inc(last, "x_mm")

            def solve(a):
                a.wait("s_ok")
                a.wait("t_ok", 10)
                a.wait("y_ok")
                for g in range(2):
                    for s in range(4):
                        last = mm(ps[:, 2 + g, P * s:P * s + P], kbg[:, 4 * g + s, :], g_S[:, 4 * g + s, :])
                    inc(last, "w_mm")
                for g in range(2):
                    for s in range(4):
                        last = mm(ps[:, g, P * s:P * s + P], g_S[:, 4 * g + s, :], vb[:, 4 * g + s, :])
                    inc(last, "vt_mm")

            def scan_read(b, s):
                if s:
                    b.wait("st_ok", 2 * s)
                    b.wait("u_ok", s)
                else:
                    b.wait("w_ok")
                    b.wait("st_zero")
                    b.last("osq", "o_n1")
                    b.last("oss_eps")
                mm(ps[0:64, 6, 256:256 + P], wT[:, s, 0:64], st[:, 0, :])
                inc(mm(ps[64:128, 6, 256:256 + P], wT[:, s, 64:128], st[:, 1, :]), "wh_mm")
                if s >= 4:
                    t = s - 4
                    if t:
                        b.wait("o_ok", t)
                    else:
                        b.wait("b_qp")
                    mm(ps[0:64, 7, P:2 * P], qp_b[:, t, 0:64], st[:, 0, :])
                    inc(mm(ps[64:128, 7, P:2 * P], qp_b[:, t, 64:128], st[:, 1, :]), "qh_mm")

            def written_u(b, s):
                b.wait("u_ok", s + 1)
                if s >= 4:
                    b.wait("qh_ok", s - 3)

            def scan_write(b, s):
                if s < STEPS - 1:
                    written_u(b, s)
                if s == 0:
                    b.wait("b_pT")
                    b.wait("b_kd")
                if s < STEPS - 1:
                    mm(ps[:, 6, 0:P], kd_b[0:64, s, :], u_buf[0:64, s % 2, :])
                    inc(mm(ps[:, 7, 0:P], kd_b[64:128, s, :], u_buf[64:128, s % 2, :]), "dh_mm")
                if s >= 4:
                    t = s - 4
                    inc(pair_mm(7, 2 * P, pT_b[:, t, :], u_buf[:, s % 2, :], P), "pu_mm")

            def output(b):
                b.wait("o_ok")
                for cidx in range(LSTEPS):
                    o = ps[:, 7, SEQ + CHUNK * cidx:SEQ + CHUNK * cidx + CHUNK]
                    mm(o, o_buf[:, cidx, :], c1[:, 0:64], True, False)
                    last = mm(o, o_buf[:, LSTEPS - 1 - cidx, :], c1[:, 64:128], False, True)
                inc(last, "oT_mm")

            def step(ha, hb, hc):
                a, b = (None if h is None else Head(pe, h) for h in (ha, hb))
                if a:
                    products_k(a)
                    token_v(a)
                    token_k(a)
                if b:
                    scan_read(b, 0)
                if a:
                    fnet_channels(a)
                if b:
                    scan_write(b, 0)
                    scan_read(b, 1)
                if a:
                    fnet_positions(a)
                if b:
                    scan_write(b, 1)
                if b:
                    scan_read(b, 2)
                if a:
                    decay_sums(a)
                if b:
                    scan_write(b, 2)
                if a:
                    products_q(a)
                if b:
                    scan_read(b, 3)
                    scan_write(b, 3)
                if a:
                    transposed(a)
                for lv in range(5):
                    for g in range(2):
                        if a:
                            y_level(a, lv, g)
                        if b and lv < 2:
                            if g == 0:
                                scan_read(b, 4 + 2 * lv)
                            else:
                                scan_write(b, 4 + 2 * lv)
                        if b and lv == 2 and g == 0:
                            output(b)
                    for g in range(2):
                        if b and lv == 2 and g == 1:
                            b.wait("osq")
                            inc(mm(ps[:, 6, 0:SEQ], ones, sq_o[:]), "oss_mm")
                        if b and lv == 1 and g == 1:
                            written_u(b, STEPS - 1)
                        if a:
                            x_level(a, lv, g)
                        if b and lv < 2:
                            if g == 0:
                                scan_read(b, 5 + 2 * lv)
                            else:
                                scan_write(b, 5 + 2 * lv)
                if a:
                    solve(a)

            run_heads(pe, step)

        @block.tensor
        def _(pe):
            def mm(o, lhsT, rhs, start, stop):
                return nc.tensor.matmul(o, lhsT, rhs, start=start, stop=stop)

            def unit_ready(seg, i, j, b):
                p = seg.pos + seg.at[j]
                w = seg.weight + j
                if b == 0:
                    pe.wait_ge(even_ready, w + 1 + len(seg.at) * i)
                else:
                    pe.wait_ge(raw_free[p % RAW_SLOTS], p // RAW_SLOTS + 2 + (len(seg.pattern) // RAW_SLOTS) * i)
                return (2 * w + b) % PART_SLOTS

            def three(o, slot, c0, act_hi, act_lo, start, stop):
                w_hi, w_lo = parts[:, slot, 0, c0:c0 + P], parts[:, slot, 1, c0:c0 + P]
                mm(o, w_hi, act_hi, start, False)
                mm(o, w_hi, act_lo, False, False)
                return mm(o, w_lo, act_hi, False, stop)

            def wide_unit(seg, i, j, b, banks, N, a):
                slot = unit_ready(seg, i, j, b)
                for nt in range(2):
                    for kk in range(4):
                        k = 8 * (j % 2) + 4 * b + kk
                        last = three(ps[:, banks[nt], 0:N], slot, 256 * kk + P * nt, a[:, 0, k, :], a[:, 1, k, :],
                                     k == 0, k == KT - 1)
                last.then_inc(units_done, 1)

            def mod_products(seg, i, n, k):
                p = seg.pos + seg.mods[n]
                slot = p % RAW_SLOTS
                pe.wait_ge(raw_landed[slot], 16 * (p // RAW_SLOTS + 1) + 16 * (len(seg.pattern) // RAW_SLOTS) * i)
                for q in range(4):
                    last = mm(ps[32 * q:32 * q + 32, 7, :], cpad[:, k, :], raw[:, slot, 512 * q:512 * q + 512],
                              k == 0, k == KT - 1)
                last.then_inc(raw_free[slot], 1)

            def transpose_mod(row):
                pe.wait_ge(mod_copied, row + 1)
                for j in range(4):
                    last = nc.tensor.transpose(ps[:, 5, P * j:P * j + P], mod_row[:, P * j:P * j + P], ident)
                last.then_inc(mod_T, 1)

            def ffn_round(seg, i, G, N, a, hp, mods):
                for j in range(8):
                    s = j // 4
                    kind = (j // 2) % 2
                    if j == 0:
                        pe.wait_ge(h_ok, 2 * G + 1)
                    if j == 2:
                        pe.wait_ge(down_added, 16 * G + 1)
                    if j == 4 and mods is not None:
                        pe.wait_ge(mod_ok, mods + 1)
                    if j == 6:
                        pe.wait_ge(silu_ok, 2 * G + 1)
                    banks = (((0, 1), (2, 3)), ((4, 5), (0, 1)))[s][kind]
                    for b in range(2):
                        wide_unit(seg, i, j, b, banks, N, a)
                    if mods is not None and seg.mods:
                        for e in range(2):
                            mod_products(seg, i, 2 * j + e, 2 * j + e)
                for j in range(8, 12):
                    for b in range(2):
                        slot = unit_ready(seg, i, j, b)
                        pe.wait_ge(h_split, 2 * G + b + 1)
                        if j == 8 and b == 0:
                            pe.wait_ge(h_ok, 2 * G + 2)
                            pe.wait_ge(silu_ok, 2 * G + 2)
                        for t in range(4):
                            bank = (2, 3, 6, 4)[t]
                            if j > 8 and b == 0:
                                pe.wait_ge(down_added, 16 * G + 4 * (j - 9) + t + 2)
                            for kk in range(2):
                                k = 2 * b + kk
                                last = three(ps[:, bank, 0:N], slot, 512 * kk + P * t, hp[:, 0, k, :],
                                             hp[:, 1, k, :], k == 0, k == GT - 1)
                            if b and t < 3:
                                last.then_inc(down_tile, 1)
                        last.then_inc(units_done, 1)
                    if j == 9 and seg.mods:
                        transpose_mod(i + 2)

            pe.wait_ge(c1_in, 16)
            pe.wait_ge(vec_in, 16 * 9)
            for v in range(N_VEC):
                nc.tensor.transpose(ps[:, 6, v * KT:(v + 1) * KT], vec_rows[:, v, :], c1[0:KT, 0:KT])
            for t in range(TAPS):
                o = N_VEC * KT + 24 * t
                last = nc.tensor.transpose(ps[:, 6, o:o + 24], conv_rows[:, t, :], c1[0:24, 0:24])
            last.then_inc(vecs_T, 1)
            pe.wait_ge(c_ok, 2)
            with pe.Fori(0, 2) as i:
                pe.wait_ge(mod_ok, i + 1)
                for k in range(KT):
                    mod_products(S_MOD, i, k, k)
                transpose_mod(i)

            def transpose_x(src, base):
                for k in range(KT):
                    if k >= 4:
                        pe.wait_ge(v_ok if base == 0 else x_ok, 2 * (k - 3) if base == 0 else k - 3)
                    for t in range(4):
                        last = nc.tensor.transpose(ps[:, k % 4, P * t:P * t + P], src[:, t, P * k:P * k + P], ident)
                    last.then_inc(xT_ok, 1)

            pe.wait_ge(x_scaled, 4)
            transpose_x(x_in, 0)
            pe.wait_ge(xn_ok, KT)
            pe.wait_ge(mod_ok, 3)
            with pe.Fori(0, S_A.iters) as i:
                ffn_round(S_A, i, i, TOK, xn, h_parts, i + 2)
            with pe.Fori(0, S_B.iters) as i:
                ffn_round(S_B, i, i + A_ROUNDS, TOK, xn, h_parts, None)

            def sum_squares(n0, N):
                for k in range(KT):
                    pe.wait_ge(sq_ok, n0 + k + 1)
                    mm(ps[:, 7, 0:N], ones, sq_buf[:, k % 2, 0:N], k == 0, k == KT - 1).then_inc(sq_used, 1)

            sum_squares(0, TOK)
            pe.wait_ge(x_re, 64)
            pe.wait_ge(down_added, 1 + 16 * ROUNDS)
            pe.wait_ge(h_ok, 1 + 2 * ROUNDS)
            for k in range(KT):
                if k >= 4:
                    pe.wait_ge(x_ok, k - 3)
                for t in range(4):
                    last = nc.tensor.transpose(ps[:, k % 4, P * t:P * t + P], x_again[:, t, P * k:P * k + P], ident)
                last.then_inc(xT_ok, 1)
                if k >= 2:
                    if k == 2:
                        pe.wait_ge(rb_ok, 2)
                    pe.wait_ge(sq_ok, KT + k - 1)
                    mm(ps[:, 7, :], ones, sq_buf[:, k % 2, :], k == 2, False).then_inc(sq_used, 1)
            for k in range(KT, KT + 2):
                pe.wait_ge(sq_ok, KT + k - 1)
                mm(ps[:, 7, :], ones, sq_buf[:, k % 2, :], False, k == KT + 1).then_inc(sq_used, 1)

            def in_pairs(seg, i, N, a, before):
                for j in range(4):
                    if j % 2 == 0:
                        pr = j // 2
                        pe.wait_ge(in_copied, before + 2 * i + pr + 1)
                    for b in range(2):
                        wide_unit(seg, i, j, b, (j // 2 * 2, j // 2 * 2 + 1), N, a)

            pe.wait_ge(xn_ok, 2 * KT)
            pe.wait_ge(x_ok, KT)
            with pe.Fori(0, S_KV.iters) as i:
                in_pairs(S_KV, i, TOK, xn, 0)
            lat = xn[:, :, :, CTX:TOK]
            for n, seg in enumerate((S_Q, S_Z, S_F)):
                with pe.Fori(0, 2) as i:
                    in_pairs(seg, i, SEQ, lat, 8 + 4 * n)
            pe.wait_ge(in_copied, 2 + 20)
            for b in range(2):
                slot = unit_ready(S_AB, 0, 0, b)
                for kk in range(8):
                    k = 8 * b + kk
                    last = three(ps[:, 0, :], slot, P * kk, xn[:, 0, k, :], xn[:, 1, k, :], k == 0, k == KT - 1)
                last.then_inc(units_done, 1)

            mixer_pe(pe)

            pe.wait_ge(hs["o_lo"], HEADS)
            pe.wait_ge(hs["f_lo"], HEADS)
            with pe.Fori(0, S_OUT.iters) as i:
                in_pairs(S_OUT, i, SEQ, xn2, 20)
            sum_squares(2 * KT, SEQ)
            pe.wait_ge(rb_ok, 4)
            sum_squares(3 * KT, SEQ)
            pe.wait_ge(xn_ok, 3 * KT)
            with pe.Fori(0, S_F2.iters) as i:
                ffn_round(S_F2, i, i + ROUNDS, SEQ, xn2, h2_parts, None)
            ffn_round(S_F2L, 0, 2 * ROUNDS - 1, SEQ, xn2, h2_parts, None)
            sum_squares(4 * KT, SEQ)
            for t in range(2):
                for q in range(4):
                    n = 4 * t + q
                    pe.wait_ge(x_ok, 2 * KT + 4 * q + 4)
                    if n == 7:
                        pe.wait_ge(rb_ok, 6)
                    for e in range(4):
                        k = 4 * q + e
                        last = nc.tensor.transpose(ps[:, n, P * e:P * e + P], acc2[:, k, P * t:P * t + P], ident)
                    last.then_inc(out_T, 1)

    return nc


_INS = ["x", "c", "ctx", "c_ctx", "w_mod", "b_mod", "g_pre", "g_post", "w1_gate", "w1_up", "w1_down", "w_in",
        "conv_w", "a_log", "dt_bias", "g_onorm", "w_out", "w2_gate", "w2_up", "w2_down"]


def kernel(**inputs):
    import concourse.bacc as _bacc
    from concourse.bass_utils import run_bass_kernel_spmd as _run

    nc = _bacc.Bacc("TRN2", target_bir_lowering=False, num_devices=1)
    arrays, args = {}, []
    for name in _INS:
        a = np.ascontiguousarray(inputs[name])
        arrays[f"in_{name}"] = a
        args.append(nc.dram_tensor(f"in_{name}", a.shape, mybir.dt.from_np(a.dtype), kind="ExternalInput").ap())
    for n, a in enumerate(shape_constants()):
        arrays[f"const{n + 1}"] = a
        args.append(nc.dram_tensor(f"const{n + 1}", a.shape, F32, kind="ExternalInput").ap())
    res = nc.dram_tensor("out_0", (1, SEQ, D), F32, kind="ExternalOutput").ap()
    build_layer(nc, *args, res)
    r = _run(nc, [arrays], core_ids=[0])
    return r.results[0]["out_0"]
```
